# Optimizing a Trainium2 kernel written in Bass

```python
import jax, jax.numpy as jnp
from jax import lax
import numpy as np

D_MODEL = 1024
BATCH = 1
SEQ = 512
DEPTH = 1
DEC_BATCH = 1
DEC_SEQ = 1024
PAST_LEN = 128

D_RWKV = 512
RWKV_HEAD = 64
RWKV_HEADS = D_RWKV // RWKV_HEAD
W_LORA = 32
A_LORA = 32
G_LORA = 96
GN_EPS = 64e-5
C_CONV = 512
CONV_W = 31
LN_EPS = 1e-5
N_BRANCHES = 2
N_EXPERTS = 16
D_FF_EXPERT = 1024
CAPACITY_FACTOR = 2
RMS_EPS = 1e-6

RWKV_COLS = 3 * D_RWKV + 2 * W_LORA + 2 * A_LORA + G_LORA
IN_COLS = RWKV_COLS + 2 * C_CONV + N_BRANCHES * D_MODEL

kernel_name = "hybrid_rwkv7_conformer_ec_moe_encoder"

def rms_norm(x, g):
    xf = x.astype(jnp.float32)
    y = xf * lax.rsqrt(jnp.mean(xf * xf, axis=-1, keepdims=True) + RMS_EPS)
    return (y * g.astype(jnp.float32)).astype(x.dtype)

def layer_norm(x, g, b):
    xf = x.astype(jnp.float32)
    mu = jnp.mean(xf, axis=-1, keepdims=True)
    var = jnp.mean(jnp.square(xf - mu), axis=-1, keepdims=True)
    y = (xf - mu) * lax.rsqrt(var + LN_EPS)
    return (y * g.astype(jnp.float32) + b.astype(jnp.float32)).astype(x.dtype)

def centred_shift(z, mu_prev, mu_next):
    zp = jnp.pad(z, ((0, 0), (1, 0), (0, 0)))[:, :-1]
    zn = jnp.pad(z, ((0, 0), (0, 1), (0, 0)))[:, 1:]
    return z + mu_prev * (zp - z) + mu_next * (zn - z)

def wkv7_scan(r, logw, k, v, a, b, reverse):
    B, T, H, N = r.shape
    decay = jnp.exp(-jnp.exp(logw.astype(jnp.float32)))
    xs = tuple(jnp.moveaxis(t.astype(jnp.float32), 1, 0) for t in (r, decay, k, v, a, b))

    def step(S, inp):
        r_t, w_t, k_t, v_t, a_t, b_t = inp
        sa = jnp.einsum('bhij,bhj->bhi', S, a_t)
        S = (S * w_t[:, :, None, :] + sa[..., :, None] * b_t[..., None, :]
             + v_t[..., :, None] * k_t[..., None, :])
        return S, jnp.einsum('bhij,bhj->bhi', S, r_t)

    S0 = jnp.zeros((B, H, N, N), jnp.float32)
    _, ys = lax.scan(step, S0, xs, reverse=reverse)
    return jnp.moveaxis(ys, 0, 1)

def rwkv7_branch(z, decay_w0, decay_up, iclr_a0, iclr_up, gate_up, k_k, k_a, r_k, lnx_w, lnx_b):
    B, T, _ = z.shape
    o = 3 * D_RWKV
    r = z[..., 0:D_RWKV]
    k = z[..., D_RWKV:2 * D_RWKV]
    v = z[..., 2 * D_RWKV:o]
    wd = z[..., o:o + 2 * W_LORA].reshape(B, T, 2, W_LORA)
    ad = z[..., o + 2 * W_LORA:o + 2 * W_LORA + 2 * A_LORA].reshape(B, T, 2, A_LORA)
    gd = z[..., o + 2 * W_LORA + 2 * A_LORA:]

    logw = -jax.nn.softplus(-(decay_w0 + jnp.einsum('btdr,drc->btdc', jnp.tanh(wd), decay_up))) - 0.5
    a = jax.nn.sigmoid(iclr_a0 + jnp.einsum('btdr,drc->btdc', ad, iclr_up))
    g = jax.nn.sigmoid(gd) @ gate_up

    heads = lambda t: t.reshape(B, T, RWKV_HEADS, RWKV_HEAD)
    kk = heads((k * k_k).astype(jnp.float32))
    kk = kk / jnp.maximum(jnp.linalg.norm(kk, axis=-1, keepdims=True), 1e-12)

    wkv = 0.0
    k_sum = 0.0
    for d, rev in ((0, False), (1, True)):
        a_d = a[:, :, d]
        k_d = k * (1.0 + (a_d - 1.0) * k_a)
        wkv = wkv + wkv7_scan(heads(r), heads(logw[:, :, d]), heads(k_d), heads(v),
                              -kk, kk * heads(a_d).astype(jnp.float32), rev)
        k_sum = k_sum + k_d

    mu = jnp.mean(wkv, axis=-1, keepdims=True)
    var = jnp.mean(jnp.square(wkv - mu), axis=-1, keepdims=True)
    y = ((wkv - mu) * lax.rsqrt(var + GN_EPS)).reshape(B, T, D_RWKV)
    y = y * lnx_w.astype(jnp.float32) + lnx_b.astype(jnp.float32)
    bonus = (jnp.sum(heads(r * k_sum * r_k.reshape(D_RWKV)), axis=-1, keepdims=True) * heads(v))
    y = (y + bonus.reshape(B, T, D_RWKV).astype(jnp.float32)) * g.astype(jnp.float32)
    return y.astype(z.dtype)

def conformer_conv_branch(u, dw_kernel, dw_bias, ln_w, ln_b):
    c = u[..., :C_CONV] * jax.nn.sigmoid(u[..., C_CONV:])
    c = lax.conv_general_dilated(
        c, dw_kernel[:, None, :].astype(c.dtype), window_strides=(1,),
        padding=[(CONV_W // 2, CONV_W // 2)],
        dimension_numbers=('NWC', 'WIO', 'NWC'),
        feature_group_count=C_CONV) + dw_bias
    return jax.nn.silu(layer_norm(c, ln_w, ln_b))

def expert_choice_ffn(h, router_w, router_b, w_gate, w_up, w_down):
    B, T, D = h.shape
    n_tok = B * T
    xf = h.reshape(n_tok, D)
    aff = jax.nn.softmax((xf @ router_w + router_b).astype(jnp.float32), axis=-1)
    cap = max(1, CAPACITY_FACTOR * n_tok // N_EXPERTS)
    gate, idx = lax.top_k(aff.T, cap)
    xe = xf[idx]
    hid = jax.nn.silu(jnp.einsum('ecd,edf->ecf', xe, w_gate)) * jnp.einsum('ecd,edf->ecf', xe, w_up)
    ye = jnp.einsum('ecf,efd->ecd', hid, w_down) * gate[..., None].astype(h.dtype)
    y = jnp.zeros((n_tok, D), h.dtype).at[idx.reshape(-1)].add(ye.reshape(-1, D).astype(h.dtype))
    return y.reshape(B, T, D)

def encoder_trunk(x, norm_mix, w_in, shift_mu_prev, shift_mu_next, decay_w0, decay_up, iclr_a0,
                  iclr_up, gate_up, k_k, k_a, r_k, lnx_w, lnx_b, w_o_rwkv, dw_kernel, dw_bias,
                  conv_ln_w, conv_ln_b, w_o_conv, w_out, norm_ffn, router_w, router_b,
                  exp_w_gate, exp_w_up, exp_w_down, norm_final):
    for l in range(DEPTH):
        h = rms_norm(x, norm_mix[l])
        p = h @ w_in[l]
        z = centred_shift(p[..., :RWKV_COLS], shift_mu_prev[l], shift_mu_next[l])
        u = p[..., RWKV_COLS:RWKV_COLS + 2 * C_CONV]
        gates = jax.nn.sigmoid(p[..., RWKV_COLS + 2 * C_CONV:])
        g_a, g_b = gates[..., :D_MODEL], gates[..., D_MODEL:]
        y_a = rwkv7_branch(z, decay_w0[l], decay_up[l], iclr_a0[l], iclr_up[l], gate_up[l],
                           k_k[l], k_a[l], r_k[l], lnx_w[l], lnx_b[l]) @ w_o_rwkv[l]
        y_b = conformer_conv_branch(u, dw_kernel[l], dw_bias[l], conv_ln_w[l], conv_ln_b[l]) @ w_o_conv[l]
        x = x + (g_a * y_a + g_b * y_b) @ w_out[l]
        x = x + expert_choice_ffn(rms_norm(x, norm_ffn[l]), router_w[l], router_b[l],
                                  exp_w_gate[l], exp_w_up[l], exp_w_down[l])
    return rms_norm(x, norm_final)

def setup_inputs(seed: int = 0) -> dict:
    key = jax.random.key(seed)
    ks = jax.random.split(key, 32)
    L, D, E, F = DEPTH, D_MODEL, N_EXPERTS, D_FF_EXPERT
    f32 = jnp.float32
    nrm = lambda k, shape, s: jax.random.normal(k, shape, f32) * s
    return {
        "x_prompt": nrm(ks[0], (BATCH, SEQ, D), 1.0),
        "x_sample": nrm(ks[1], (DEC_BATCH, DEC_SEQ, D), 1.0),
        "norm_mix": 1.0 + nrm(ks[2], (L, D), 0.05),
        "w_in": nrm(ks[3], (L, D, IN_COLS), D ** -0.5),
        "shift_mu_prev": jax.random.uniform(ks[4], (L, RWKV_COLS), f32, 0.0, 0.5),
        "shift_mu_next": jax.random.uniform(ks[5], (L, RWKV_COLS), f32, 0.0, 0.5),
        "decay_w0": jax.random.uniform(ks[6], (L, 2, D_RWKV), f32, -5.0, -1.0),
        "decay_up": nrm(ks[7], (L, 2, W_LORA, D_RWKV), 0.1),
        "iclr_a0": nrm(ks[8], (L, 2, D_RWKV), 0.1),
        "iclr_up": nrm(ks[9], (L, 2, A_LORA, D_RWKV), 0.1),
        "gate_up": nrm(ks[10], (L, G_LORA, D_RWKV), G_LORA ** -0.5),
        "k_k": 0.85 + nrm(ks[11], (L, D_RWKV), 0.05),
        "k_a": 1.0 + nrm(ks[12], (L, D_RWKV), 0.05),
        "r_k": nrm(ks[13], (L, RWKV_HEADS, RWKV_HEAD), 0.1),
        "lnx_w": 1.0 + nrm(ks[14], (L, D_RWKV), 0.05),
        "lnx_b": nrm(ks[15], (L, D_RWKV), 0.02),
        "w_o_rwkv": nrm(ks[16], (L, D_RWKV, D), D_RWKV ** -0.5),
        "dw_kernel": nrm(ks[17], (L, CONV_W, C_CONV), CONV_W ** -0.5),
        "dw_bias": nrm(ks[18], (L, C_CONV), 0.02),
        "conv_ln_w": 1.0 + nrm(ks[19], (L, C_CONV), 0.05),
        "conv_ln_b": nrm(ks[20], (L, C_CONV), 0.02),
        "w_o_conv": nrm(ks[21], (L, C_CONV, D), C_CONV ** -0.5),
        "w_out": nrm(ks[22], (L, D, D), D ** -0.5),
        "norm_ffn": 1.0 + nrm(ks[23], (L, D), 0.05),
        "router_w": nrm(ks[24], (L, D, E), D ** -0.5),
        "router_b": nrm(ks[25], (L, E), 0.01),
        "exp_w_gate": nrm(ks[26], (L, E, D, F), D ** -0.5),
        "exp_w_up": nrm(ks[27], (L, E, D, F), D ** -0.5),
        "exp_w_down": nrm(ks[28], (L, E, F, D), F ** -0.5),
        "norm_final": 1.0 + nrm(ks[29], (D,), 0.05),
    }

def reference(x_prompt, x_sample, norm_mix, w_in, shift_mu_prev, shift_mu_next, decay_w0, decay_up,
              iclr_a0, iclr_up, gate_up, k_k, k_a, r_k, lnx_w, lnx_b, w_o_rwkv, dw_kernel, dw_bias,
              conv_ln_w, conv_ln_b, w_o_conv, w_out, norm_ffn, router_w, router_b, exp_w_gate,
              exp_w_up, exp_w_down, norm_final):
    params = (norm_mix, w_in, shift_mu_prev, shift_mu_next, decay_w0, decay_up, iclr_a0, iclr_up,
              gate_up, k_k, k_a, r_k, lnx_w, lnx_b, w_o_rwkv, dw_kernel, dw_bias, conv_ln_w,
              conv_ln_b, w_o_conv, w_out, norm_ffn, router_w, router_b, exp_w_gate, exp_w_up,
              exp_w_down, norm_final)
    y_prompt = encoder_trunk(x_prompt, *params)
    y_sample = encoder_trunk(x_sample, *params)
    return (y_prompt, y_sample)


_drawn_inputs = setup_inputs


def setup_inputs(seed=0):
    import zlib

    import numpy as np

    out = dict(_drawn_inputs(seed))
    spreads = {}
    factors = {'decay_up': 4.592,
     'iclr_a0': 3.725,
     'k_k': 3.644,
     'k_a': 2.898,
     'lnx_w': 3.434,
     'lnx_b': 7.835,
     'dw_bias': 4.051,
     'conv_ln_b': 5.72,
     'router_b': 25.484,
     'conv_ln_w': 3.485,
     'norm_ffn': 2.703}
    for name, (base, spread) in spreads.items():
        noise = np.random.default_rng([zlib.crc32(name.encode()), seed]).standard_normal(out[name].shape)
        drawn = base * np.exp(spread * noise) if base else spread * noise
        out[name] = __import__('jax').numpy.asarray(drawn.astype(out[name].dtype))
    for name, factor in factors.items():
        out[name] = (out[name] * factor).astype(out[name].dtype)
    return out
```

```python
import numpy as np
import concourse.bass as bass
from concourse import mybir
from contextlib import ExitStack

F32 = mybir.dt.float32
U32 = mybir.dt.uint32
F32R = mybir.dt.float32r
ALU = mybir.AluOpType
ACT = mybir.ActivationFunctionType
AXIS = mybir.AxisListType

P = 128
D = 1024
KD = D // P
T_PROMPT, T_SAMPLE = 512, 1024
T = T_PROMPT + T_SAMPLE
BLK = 512
NB = T // BLK
DR = 512
HEADS, HD = 8, 64
HP = DR // P
LORA = 32
GLORA = 96
RWKV_COLS = 3 * DR + 4 * LORA + GLORA
CC = 512
CT = CC // P
TAPS = 31
PAD = TAPS // 2
E = 16
FF = 1024
CAP = [2 * T_PROMPT // E, 2 * T_SAMPLE // E]
CH = 64
NCH = T // CH
KAPPA = float(np.exp(-0.5))
GN_EPS, LN_EPS, RMS_EPS, KK_EPS = 64e-5, 1e-5, 1e-6, 1e-12
GROUPS = [(0, T_PROMPT), (T_PROMPT, T)]

N_CONV, N_GATE, N_TILES = 2 * CT, 2 * KD, 38
T_GATE = N_CONV
T_LORA = T_GATE + N_GATE
T_RKV = T_LORA + 2

VEC = {}
_at = 0
for _name, _n in (("norm_mix", KD), ("mu_prev", 14), ("mu_next", 14), ("k_k", HP), ("k_a", HP), ("r_k", HP),
                  ("lnx_w", HP), ("lnx_b", HP), ("dw_bias", CT), ("conv_ln_w", CT), ("conv_ln_b", CT),
                  ("dw_kernel", CT * TAPS)):
    VEC[_name] = (_at, _n)
    _at += _n
N_VEC = _at

CON = {}
_at = 0
for _name, _n in (("ident", P), ("pair_sum", P), ("ones", P), ("ident_pair", HD), ("eps", 4)):
    CON[_name] = (_at, _n)
    _at += _n
N_CON = _at
for _name, _n in (("mask_n", 2 * HD), ("mask_nt", 2 * HD), ("mask_y", 2 * HD), ("level", 2 * 6 * HD),
                  ("level_t", 2 * HD), ("keep", 2 * NCH), ("reset", 4 * CH)):
    CON[_name] = (_at, _n)
    _at += _n
N_CON_ALL = _at


def constants():
    c = np.zeros((P, N_CON_ALL), np.float32)

    def put(name, value, at=0):
        a, _ = CON[name]
        c[:, a + at:a + at + value.shape[1]] = value

    put("ident", np.eye(P))
    put("pair_sum", np.kron(np.eye(2), np.ones((HD, HD))))
    put("ones", np.ones((P, P)))
    put("ident_pair", np.tile(np.eye(HD), (2, 1)))
    put("eps", np.tile(np.array([[RMS_EPS, GN_EPS, LN_EPS, 0.0]]), (P, 1)))
    t = np.arange(HD)
    for d in range(2):
        after = t[:, None] > t[None, :] if d == 0 else t[:, None] < t[None, :]
        put("mask_n", np.tile(after, (2, 1)), d * HD)
        put("mask_nt", np.tile(after.T, (2, 1)), d * HD)
        put("mask_y", np.tile(after.T | np.eye(HD, dtype=bool), (2, 1)), d * HD)
        for n in range(6):
            b = 1 << n
            row, col = t[:, None] // b, t[None, :] // b
            m = (row % 2 == 1) & (col == row - 1) if d == 0 else (row % 2 == 0) & (col == row + 1)
            put("level", np.tile(m, (2, 1)), (d * 6 + n) * HD)
            if n == 0:
                put("level_t", np.tile(m.T, (2, 1)), d * HD)
        keep = np.ones((P, NCH))
        keep[:, (T_PROMPT // CH - 1) if d == 0 else (T_SAMPLE // CH - 1)] = 0
        put("keep", keep, d * NCH)
    put("reset", np.tile((np.arange(4 * CH) % CH != 0).astype(np.float32), (P, 1)))
    return c


def apart(eng, g, sem, value):
    eng.wait_ge(sem, value)
    if not isinstance(value, int):
        eng.sem_inc(g.passed, 1)


class Chain:

    def __init__(self, eng, sem):
        self.eng, self.sem, self.base, self.n = eng, sem, 0, 0

    def count(self, ins):
        self.n += 1
        return ins.then_inc(self.sem, 1)

    def wait(self):
        self.eng.wait_ge(self.sem, self.base + self.n)

    def link(self, ins):
        self.count(ins)
        self.wait()

    def begin(self):
        self.origin = self.base + self.n

    def enter(self, i, per):
        self.base, self.n, self.per = self.origin + i * per, 0, per

    def leave(self, times):
        assert self.n == self.per, f"{self.n} steps"
        self.base, self.n = self.origin + times * self.per, 0


def repeat(eng, times, step, last=None):
    step(0)
    with eng.Fori(1, times if last is None else times - 1) as i:
        step(i)
    if last is not None:
        last(times - 1)


def allocate(nc, ctx, g):
    g.sb = lambda name, shape, dt=F32: ctx.enter_context(nc.sbuf_tensor(name, shape, dt))
    g.bank = [ctx.enter_context(nc.psum_tensor(f"bank{i}", [P, BLK], F32)) for i in range(8)]
    g.con = g.sb("con", [P, N_CON])
    g.vec = g.sb("vec", [P, N_VEC])

    def con(name, at=0, n=None, rows=slice(0, P)):
        a, full = CON[name]
        return g.con[rows, a + at:a + at + (full if n is None else n)]

    def vec(name, i=0, rows=slice(0, P)):
        a, _ = VEC[name]
        return g.vec[rows, a + i:a + i + 1]

    g.c, g.v = con, vec
    g.gates = nc.dram_tensor("gates_dram", (2 * D, T), F32).ap()
    g.conv_dram = nc.dram_tensor("conv_dram", (P, CT, T), F32).ap()
    g.sg_dram = nc.dram_tensor("sg_dram", (GLORA, T), F32).ap()
    g.mix = nc.dram_tensor("mix_dram", (KD, P, T), F32).ap()
    g.xacc = nc.dram_tensor("xacc_dram", (T, D), F32).ap()
    g.h2 = nc.dram_tensor("h2_dram", (T, D), F32).ap()
    g.s_const = ctx.enter_context(nc.semaphore("s_const"))
    g.passed = ctx.enter_context(nc.semaphore("s_passed"))


def project(nc, a, g):
    with ExitStack() as ctx:
        sb = lambda name, shape, dt=F32: ctx.enter_context(nc.sbuf_tensor(name, shape, dt))
        sem = nc.alloc_semaphore
        h = sb("h", [P, KD, T])
        w = [sb(f"w{j}", [P, KD, P]) for j in range(2)]
        stage = [sb(f"stage{j}", [P, T + 3]) for j in range(2)]
        cin = sb("cin", [P, T + 3 * PAD])
        acc = sb("acc", [P, T + PAD])
        tmp = sb("tmp", [P, T])
        mu_own = sb("mu_own", [P, 14])
        conv = sb("conv", [P, CT, T])
        sg = sb("sg", [GLORA, T])
        zl = acc[:, 0:T]
        zg = cin[:, 0:T]
        n_acc = T + PAD

        x_in = [sem(f"p_x_in{k}") for k in range(KD)]
        squared, summed, rooted, normed = sem("p_squared"), sem("p_summed"), sem("p_rooted"), sem("p_normed")
        w_in = [sem(f"p_w_in{j}") for j in range(2)]
        projected = [sem(f"p_projected{j}") for j in range(2)]
        evacuated = [sem(f"p_evacuated{j}") for j in range(2)]
        stage_used = [sem(f"p_stage_used{j}") for j in range(2)]
        gate_out = [sem(f"p_gate_out{j}") for j in range(2)]
        padded, shifted, lora_done = sem("p_padded"), sem("p_shifted"), sem("p_lora_done")
        dve_step, spilled = sem("p_dve_step"), sem("p_spilled")

        with nc.Block() as block:
            @block.sync
            def _(sp):
                sp.dma_start(g.con[:], a["con"][:, 0:N_CON]).then_inc(g.s_const, 16)
                sp.dma_start(g.vec[:], a["vec"]).then_inc(g.s_const, 16)
                for k in range(KD):
                    sp.dma_start(h[:, k, :], a["xT"][:, k, :]).then_inc(x_in[k], 16)
                def load(i):
                    for j in range(2):
                        sp.wait_ge(projected[j], i)
                        sp.dma_start(w[j][:].rearrange("p k c -> p (k c)"), a["w_in"][2 * i + j, :, :])\
                          .then_inc(w_in[j], 16)

                repeat(sp, N_TILES // 2, load)
                sp.wait_ge(padded, 1)
                sp.dma_start(g.conv_dram, conv[:]).then_inc(spilled, 16)
                sp.wait_ge(lora_done, 1)
                sp.dma_start(g.sg_dram, sg[:]).then_inc(spilled, 16)
                sp.wait_ge(spilled, 32)

            @block.tensor
            def _(pe):
                pe.wait_ge(g.s_const, 32)
                for k in range(KD):
                    pe.wait_ge(squared, k + 1)
                    for b in range(NB):
                        mm = nc.tensor.matmul(g.bank[b][:], g.c("ones"), stage[k % 2][:, b * BLK:(b + 1) * BLK],
                                              start=(k == 0), stop=(k == KD - 1))
                    mm.then_inc(summed, 1)
                pe.wait_ge(normed, KD)
                def tiles(i):
                    for j in range(2):
                        pe.wait_ge(w_in[j], i * 16 + 16)
                        pe.wait_ge(evacuated[j], i)
                        for k in range(KD):
                            for b in range(NB):
                                mm = nc.tensor.matmul(g.bank[3 * j + b][:], w[j][:, k, :],
                                                      h[:, k, b * BLK:(b + 1) * BLK],
                                                      start=(k == 0), stop=(k == KD - 1))
                        mm.then_inc(projected[j], 1)

                repeat(pe, N_TILES // 2, tiles)

            @block.scalar
            def _(act):
                for k in range(KD):
                    act.wait_ge(x_in[k], 16)
                    if k >= 2:
                        act.wait_ge(summed, k - 1)
                    nc.scalar.activation(stage[k % 2][:, 0:T], h[:, k, :], ACT.Square).then_inc(squared, 1)
                act.wait_ge(summed, KD)
                for b in range(NB):
                    nc.scalar.activation(tmp[:, b * BLK:(b + 1) * BLK], g.bank[b][:], ACT.Sqrt,
                                         bias=g.c("eps", 0, 1), scale=1.0 / D).then_inc(rooted, 1)

                def evacuate(j, i, func, skip):
                    act.wait_ge(projected[j], i + 1)
                    act.wait_ge(stage_used[j], i)
                    for b in range(NB):
                        at = b * BLK + (skip if b == 0 else 2 * skip)
                        ins = nc.scalar.activation(stage[j][:, at:at + BLK], g.bank[3 * j + b][:], func)
                    ins.then_inc(evacuated[j], 1)

                def conv_pair(i):
                    evacuate(0, i, ACT.Copy, 0)
                    evacuate(1, i, ACT.Sigmoid, 0)

                def gate_pair(n):
                    for j in range(2):
                        i = n + T_GATE // 2
                        act.wait_ge(stage_used[j], CT)
                        act.wait_ge(gate_out[j], n * 16)
                        act.wait_ge(projected[j], i + 1)
                        for b in range(NB):
                            ins = nc.scalar.activation(stage[j][:, b * BLK:(b + 1) * BLK],
                                                       g.bank[3 * j + b][:], ACT.Sigmoid)
                        ins.then_inc(evacuated[j], 1)
                        act.wait_ge(evacuated[j], i + 1)
                        act.dma_start(g.gates[bass.ds((2 * n + j) * P, P), :], stage[j][:, 0:T])\
                           .then_inc(gate_out[j], 16)

                repeat(act, N_CONV // 2, conv_pair)
                repeat(act, N_GATE // 2, gate_pair)
                for j in range(2):
                    act.wait_ge(gate_out[j], 16 * N_GATE // 2)
                act.wait_ge(padded, 2)
                done = N_CONV // 2

                def raw(j, i, used):
                    act.wait_ge(projected[j], i + 1)
                    act.wait_ge(stage_used[j], used)
                    for b in range(NB):
                        at = b * BLK + (1 if b == 0 else 2)
                        ins = nc.scalar.activation(stage[j][:, at:at + BLK], g.bank[3 * j + b][:], ACT.Copy)
                    ins.then_inc(evacuated[j], 1)

                raw(0, T_LORA // 2, done)
                raw(1, T_LORA // 2, done)
                act.wait_ge(shifted, 1)
                nc.scalar.activation(g.lw[0:2 * LORA, :], zl[0:2 * LORA, :], ACT.Tanh)
                nc.scalar.activation(g.la[0:2 * LORA, :], zl[2 * LORA:4 * LORA, :], ACT.Copy)
                act.wait_ge(shifted, 2)
                nc.scalar.activation(sg[:], zg[0:GLORA, :], ACT.Sigmoid).then_inc(lora_done, 1)
                with act.Fori(0, (N_TILES - T_RKV) // 2) as i:
                    raw(0, i + T_RKV // 2, i + (done + 1))
                    raw(1, i + T_RKV // 2, i + (done + 1))

            @block.vector
            def _(dve):
                ch = Chain(dve, dve_step)
                nc.vector.memset(g.lw[2 * LORA:2 * LORA + 1, :], 1.0)
                nc.vector.memset(g.la[2 * LORA:2 * LORA + 1, :], 1.0)
                ch.link(nc.vector.memset(cin[:], 0.0))
                dve.wait_ge(g.s_const, 32)
                ch.link(nc.vector.tensor_tensor(mu_own[:], g.vec[:, VEC["mu_prev"][0]:VEC["mu_prev"][0] + 14],
                                                g.vec[:, VEC["mu_next"][0]:VEC["mu_next"][0] + 14], ALU.add))
                ch.link(nc.vector.tensor_scalar(mu_own[:], mu_own[:], -1.0, 1.0, ALU.mult, ALU.add))
                dve.wait_ge(rooted, NB)
                ch.link(nc.vector.reciprocal(acc[:, 0:T], tmp[:]))
                for k in range(KD):
                    nc.vector.scalar_tensor_tensor(h[:, k, :], h[:, k, :], g.v("norm_mix", k), acc[:, 0:T],
                                                   ALU.mult, ALU.mult).then_inc(normed, 1)
                dve.wait_ge(normed, KD)
                kern = VEC["dw_kernel"][0]
                bias = VEC["dw_bias"][0]
                ch.begin()
                with dve.Fori(0, CT) as i:
                    ch.enter(i, TAPS + 3)
                    dve.wait_ge(evacuated[0], i + 1)
                    dve.wait_ge(evacuated[1], i + 1)
                    ch.count(nc.vector.tensor_tensor(cin[:, PAD:PAD + T_PROMPT], stage[0][:, 0:T_PROMPT],
                                                     stage[1][:, 0:T_PROMPT], ALU.mult))
                    ch.link(nc.vector.tensor_tensor(cin[:, 2 * PAD + T_PROMPT:2 * PAD + T],
                                                    stage[0][:, T_PROMPT:T], stage[1][:, T_PROMPT:T], ALU.mult))
                    for j in range(2):
                        dve.sem_inc(stage_used[j], 1)
                    for tap in range(TAPS - 1):
                        wt = g.vec[:, bass.ds(i * TAPS + (kern + tap), 1)]
                        if tap == 0:
                            ch.link(nc.vector.tensor_scalar(acc[:], cin[:, 0:n_acc], wt,
                                                            g.vec[:, bass.ds(i + bias, 1)], ALU.mult, ALU.add))
                        else:
                            ch.link(nc.vector.scalar_tensor_tensor(acc[:], cin[:, tap:tap + n_acc], wt, acc[:],
                                                                   ALU.mult, ALU.add))
                    wt = g.vec[:, bass.ds(i * TAPS + (kern + TAPS - 1), 1)]
                    for lo, hi, shift in ((0, T_PROMPT, 0), (T_PROMPT, T, PAD)):
                        ins = nc.vector.scalar_tensor_tensor(
                            conv[:, i, lo:hi], cin[:, lo + shift + TAPS - 1:hi + shift + TAPS - 1], wt,
                            acc[:, lo + shift:hi + shift], ALU.mult, ALU.add)
                        ch.count(ins)
                    ch.wait()
                ch.leave(CT)
                for j in range(2):
                    dve.wait_ge(gate_out[j], 16 * N_GATE // 2)
                    for at in (0, T_PROMPT + 1, T + 2):
                        ins = nc.vector.memset(stage[j][:, at:at + 1], 0.0)
                    ins.then_inc(padded, 1)

                def shift(j, n, out, ready):
                    dve.wait_ge(evacuated[j], ready)
                    zp, zn = VEC["mu_prev"][0], VEC["mu_next"][0]
                    at = lambda first: (g.vec[:, bass.ds(n + first, 1)])
                    for part in range(3):
                        for lo, hi, s in ((0, T_PROMPT, 0), (T_PROMPT, T, 1)):
                            src = stage[j][:, lo + s + (1, 0, 2)[part]:hi + s + (1, 0, 2)[part]]
                            if part == 0:
                                ins = nc.vector.tensor_scalar(tmp[:, lo:hi], src, mu_own[:, bass.ds(n, 1)],
                                                              None, ALU.mult)
                            elif part == 1:
                                ins = nc.vector.scalar_tensor_tensor(tmp[:, lo:hi], src, at(zp), tmp[:, lo:hi],
                                                                     ALU.mult, ALU.add)
                            else:
                                ins = nc.vector.scalar_tensor_tensor(out[:, lo:hi], src, at(zn), tmp[:, lo:hi],
                                                                     ALU.mult, ALU.add)
                            ch.count(ins)
                        ch.wait()
                    dve.sem_inc(stage_used[j], 1)

                shift(0, 0, zl, T_LORA // 2 + 1)
                dve.sem_inc(shifted, 1)
                shift(1, 1, zg, T_LORA // 2 + 1)
                dve.sem_inc(shifted, 1)
                ch.begin()
                with dve.Fori(0, (N_TILES - T_RKV) // 2) as i:
                    ch.enter(i, 12)
                    for j in range(2):
                        shift(j, 2 * i + (2 + j), g.rkv[:, 2 * i + j, :], i + (T_RKV // 2 + 1))
                ch.leave((N_TILES - T_RKV) // 2)


def normalise_keys(nc, a, g):
    with ExitStack() as ctx:
        sb = lambda name, shape, dt=F32: ctx.enter_context(nc.sbuf_tensor(name, shape, dt))
        sem = nc.alloc_semaphore
        sq = [sb(f"kk_sq{j}", [P, T]) for j in range(2)]
        nrm = [sb(f"kk_nrm{j}", [P, T]) for j in range(2)]
        scaled, squared, summed, rooted = (sem("k_scaled"), sem("k_squared"), sem("k_summed"), sem("k_rooted"))
        dve_step = sem("k_dve_step")
        with nc.Block() as block:
            @block.vector
            def _(dve):
                ch = Chain(dve, dve_step)
                ch.count(nc.vector.memset(g.y[:], 0.0))
                for hp in range(HP):
                    nc.vector.tensor_scalar(g.nkk[:, hp, :], g.rkv[:, HP + hp, :], g.v("k_k", hp), None, ALU.mult)\
                      .then_inc(scaled, 1)
                for hp in range(HP):
                    dve.wait_ge(rooted, NB * (hp + 1))
                    ch.link(nc.vector.tensor_scalar(nrm[hp % 2][:], nrm[hp % 2][:], KK_EPS, None, ALU.max))
                    ch.link(nc.vector.reciprocal(nrm[hp % 2][:], nrm[hp % 2][:]))
                    ch.link(nc.vector.scalar_tensor_tensor(g.nkk[:, hp, :], g.nkk[:, hp, :], -1.0,
                                                           nrm[hp % 2][:], ALU.mult, ALU.mult))

            @block.scalar
            def _(act):
                for hp in range(HP):
                    act.wait_ge(scaled, hp + 1)
                    if hp >= 2:
                        act.wait_ge(summed, hp - 1)
                    nc.scalar.activation(sq[hp % 2][:], g.nkk[:, hp, :], ACT.Square).then_inc(squared, 1)
                    act.wait_ge(summed, hp + 1)
                    if hp >= 2:
                        act.wait_ge(dve_step, 1 + 3 * (hp - 1))
                    for b in range(NB):
                        nc.scalar.activation(nrm[hp % 2][:, b * BLK:(b + 1) * BLK],
                                             g.bank[3 * (hp % 2) + b][:], ACT.Sqrt).then_inc(rooted, 1)

            @block.tensor
            def _(pe):
                for hp in range(HP):
                    pe.wait_ge(squared, hp + 1)
                    if hp >= 2:
                        pe.wait_ge(rooted, NB * (hp - 1))
                    for b in range(NB):
                        mm = nc.tensor.matmul(g.bank[3 * (hp % 2) + b][:], g.c("pair_sum"),
                                              sq[hp % 2][:, b * BLK:(b + 1) * BLK], start=True, stop=True)
                    mm.then_inc(summed, 1)

            @block.sync
            def _(sp):
                sp.dma_start(g.masks[:], a["con"][:, N_CON:N_CON_ALL]).then_inc(g.s_const, 16)
                sp.dma_start(g.upw[:], a["up_w"]).then_inc(g.s_const, 16)
                sp.dma_start(g.upa[:], a["up_a"]).then_inc(g.s_const, 16)


def scan(nc, a, g):
    DIRS = range(2)
    L4 = range(HP)
    ROWS = [slice(0, HD), slice(HD, P)]
    with ExitStack() as ctx:
        sb = lambda name, shape, dt=F32: ctx.enter_context(nc.sbuf_tensor(name, shape, dt))
        sem = nc.alloc_semaphore
        two = lambda name, shape: [sb(f"{name}{d}", shape) for d in DIRS]
        sems = lambda name: [sem(f"{name}{d}") for d in DIRS]
        SG = two("sg_", [P, 2, HP, CH])
        OM = two("om", [P, HP, CH])
        WX = two("wx", [P, 3, HP, CH])
        AR = two("ar", [P, HP, 2, CH])
        BK = two("bk", [P, HP, 2, CH])
        BH = two("bh", [P, HP, CH])
        KH = two("kh", [P, HP, CH])
        VC = two("vc", [P, HP, CH])
        AM = two("am", [P, HP, 2 * CH])
        RB = two("rb", [P, HP, 2 * CH])
        FU = two("fu", [P, HP, 2, 2 * CH])
        NT = two("nt", [P, HP, CH])
        XX = two("xx", [P, HP, 2, CH])
        T1 = two("t1_", [P, HP, CH])
        GH = two("gh", [P, HP, 2 * CH])
        ST = two("st", [P, HP, 2, HD])

        m_lora, m_t1, m_t2, m_a, m_b, m_c = (sems(f"m_{n}") for n in ("lora", "t1", "t2", "a", "b", "c"))
        m_n, m_x, m_g, m_f, m_s = (sems(f"m_{n}") for n in ("n", "x", "g", "f", "s"))
        v_sum, v_prep, v_b, v_c, v_n, v_x, v_f, v_s = (
            sems(f"v_{n}") for n in ("sum", "prep", "b", "c", "n", "x", "f", "s"))
        p_v = sems("p_v")
        a_th, a_e0, a_exp, a_t1, a_t2, a_r, a_g = (sems(f"a_{n}") for n in ("th", "e0", "exp", "t1", "t2", "r", "g"))
        dve_step, pool_step = sem("s_dve_step"), sem("s_pool_step")
        bank = lambda d, n: g.bank[4 * d + n]
        LEVELS = 5

        def col(d, i):
            return i * CH if d == 0 else (NCH - 1) * CH - i * CH

        def cat(tile):
            return tile.rearrange("p h c -> p (h c)")

        def mask(name, d, n=1, at=0, rows=slice(0, P), times=HP):
            base, _ = CON[name]
            lo = base - N_CON + d * n * HD + at * HD
            return g.masks[rows, lo:lo + HD].unsqueeze(1).to_broadcast([rows.stop - rows.start, times, HD])

        with nc.Block() as block:
            @block.tensor
            def _(pe):
                apart(pe, g, g.s_const, 80)

                def lora(d, i):
                    for n, (up, act_) in enumerate(((g.upw, g.lw), (g.upa, g.la))):
                        for hp in L4:
                            at = (n * HP + hp) * CH
                            mm = nc.tensor.matmul(bank(d, 3)[:, at:at + CH], up[:, d, hp, :],
                                                  act_[:, bass.ds(col(d, i), CH)], start=True, stop=True)
                    mm.then_inc(m_lora[d], 1)

                def turn1(d, i):
                    apart(pe, g, v_prep[d], i + 1)
                    apart(pe, g, v_s[d], i)
                    for n, src in ((1, None), (2, BH[d])):
                        for hp in L4:
                            s = AR[d][:, hp, 0, :] if src is None else src[:, hp, :]
                            mm = nc.tensor.transpose(bank(d, n)[0:CH, hp * P:(hp + 1) * P], s, g.c("ident"))
                    mm.then_inc(m_t1[d], 1)

                def turn2(d, i):
                    apart(pe, g, v_f[d], i)
                    apart(pe, g, p_v[d], i + 1)
                    for n, src in ((0, KH[d]), (3, VC[d])):
                        for hp in L4:
                            mm = nc.tensor.transpose(bank(d, n)[0:CH, hp * P:(hp + 1) * P], src[:, hp, :],
                                                     g.c("ident"))
                    mm.then_inc(m_t2[d], 1)

                def products(d, i):
                    apart(pe, g, a_t1[d], i + 1)
                    for hp in L4:
                        for r in ROWS:
                            mm = nc.tensor.matmul(bank(d, 1)[r, hp * P:(hp + 1) * P], BK[d][r, hp, 0, :],
                                                  AR[d][r, hp, :, :], start=True, stop=True)
                    mm.then_inc(m_a[d], 1)
                    for hp in L4:
                        for r in ROWS:
                            mm = nc.tensor.matmul(bank(d, 2)[r, hp * P:(hp + 1) * P], AR[d][r, hp, 0, :],
                                                  BK[d][r, hp, :, :], start=True, stop=True)
                    mm.then_inc(m_b[d], 1)
                    apart(pe, g, a_t2[d], i + 1)
                    for hp in L4:
                        for par, r in enumerate(ROWS):
                            mm = nc.tensor.matmul(bank(d, (3, 0)[par])[HD:P, hp * CH:(hp + 1) * CH], BK[d][r, hp, 1, :],
                                                  AR[d][r, hp, 1, :], start=True, stop=True)
                    mm.then_inc(m_c[d], 1)

                def level_n(d, i, n):
                    if n == 0:
                        apart(pe, g, v_c[d], i + 1)
                    else:
                        apart(pe, g, v_x[d], i * LEVELS + n)
                    for r in ROWS:
                        for hp in L4:
                            mm = nc.tensor.matmul(bank(d, 0)[r, hp * CH:(hp + 1) * CH], NT[d][r, hp, :],
                                                  XX[d][r, hp, 0, :], start=True, stop=True)
                    mm.then_inc(m_n[d], 1)

                def level_x(d, i, n):
                    apart(pe, g, v_n[d], i * LEVELS + (n + 1))
                    for r in ROWS:
                        for hp in L4:
                            at = 2 * hp * CH
                            mm = nc.tensor.matmul(bank(d, 1)[r, at:at + CH], XX[d][r, hp, 1, :], T1[d][r, hp, :],
                                                  start=True, stop=True)
                            if n < LEVELS - 1:
                                mm = nc.tensor.matmul(bank(d, 1)[r, at + CH:at + 2 * CH], T1[d][r, hp, :],
                                                      XX[d][r, hp, 1, :], start=True, stop=True)
                    mm.then_inc(m_x[d], 1)

                def solve(d, i):
                    apart(pe, g, v_x[d], i * LEVELS + LEVELS)
                    for r in ROWS:
                        for hp in L4:
                            mm = nc.tensor.matmul(bank(d, 2)[r, hp * P:(hp + 1) * P], XX[d][r, hp, 0, :],
                                                  RB[d][r, hp, :], start=True, stop=True)
                    mm.then_inc(m_g[d], 1)

                def full(d, i):
                    apart(pe, g, a_g[d], i + 1)
                    apart(pe, g, v_c[d], i + 1)
                    for par, r in enumerate(ROWS):
                        for hp in L4:
                            mm = nc.tensor.matmul(bank(d, (0, 3)[par])[:, hp * P:(hp + 1) * P], AM[d][r, hp, :],
                                                  GH[d][r, hp, :], start=True, stop=True)
                    mm.then_inc(m_f[d], 1)

                def state(d, i):
                    apart(pe, g, v_f[d], i + 1)
                    for hp in L4:
                        for par, r in enumerate(ROWS):
                            mm = nc.tensor.matmul(bank(d, 1)[r, hp * CH:(hp + 1) * CH], ST[d][:, hp, par, :],
                                                  FU[d][:, hp, par, 0:CH], start=True, stop=True)
                            at = (2 * hp + par) * CH
                            mm = nc.tensor.matmul(bank(d, 2)[0:HD, at:at + CH], FU[d][:, hp, par, CH:2 * CH],
                                                  ST[d][:, hp, par, :], start=True, stop=True)
                    mm.then_inc(m_s[d], 1)

                def chunk(i, following):
                    for d in DIRS:
                        turn1(d, i)
                    for d in DIRS:
                        turn2(d, i)
                    for d in DIRS:
                        products(d, i)
                    for n in range(LEVELS):
                        for d in DIRS:
                            level_n(d, i, n)
                        for d in DIRS:
                            level_x(d, i, n)
                        if n == 0 and following is not None:
                            for d in DIRS:
                                apart(pe, g, v_c[d], i + 1)
                                lora(d, following)
                    for d in DIRS:
                        solve(d, i)
                    for d in DIRS:
                        if following is not None:
                            apart(pe, g, a_th[d], i + 2)
                        full(d, i)
                    for d in DIRS:
                        state(d, i)

                for d in DIRS:
                    lora(d, 0)
                repeat(pe, NCH, lambda i: chunk(i, i + 1), lambda i: chunk(i, None))

            @block.scalar
            def _(act):
                def copy(out, in_):
                    return nc.scalar.activation(out, in_, ACT.Copy)

                def tanh(d, i):
                    act.wait_ge(m_lora[d], i + 1)
                    act.wait_ge(v_prep[d], i)
                    nc.scalar.activation(SG[d][:].rearrange("p n h c -> p (n h c)"), bank(d, 3)[:], ACT.Tanh,
                                         scale=0.5).then_inc(a_th[d], 1)

                def exps(d, i):
                    act.wait_ge(v_sum[d], i + 1)
                    w = WX[d][:].rearrange("p n h c -> p n (h c)")
                    nc.scalar.activation(w[:, 2, :], w[:, 0, :], ACT.Exp, scale=KAPPA).then_inc(a_e0[d], 1)
                    act.wait_ge(a_e0[d], i + 1)
                    nc.scalar.activation(w[:, 0:2, :], w[:, 0:2, :], ACT.Exp, scale=-KAPPA).then_inc(a_exp[d], 1)

                def turned1(d, i):
                    act.wait_ge(m_t1[d], i + 1)
                    act.wait_ge(m_f[d], i)
                    for n, out, at in ((1, AM[d], 0), (2, RB[d], CH)):
                        src = bank(d, n)[0:CH, :].rearrange("p (h r c) -> p h r c", r=2, c=CH)
                        for par, r in enumerate(ROWS):
                            ins = copy(out[r, :, at:at + CH], src[:, :, par, :])
                    ins.then_inc(a_t1[d], 1)

                def turned2(d, i):
                    act.wait_ge(m_t2[d], i + 1)
                    act.wait_ge(m_s[d], i)
                    as8 = lambda b: b[0:CH, :].rearrange("p (h c) -> p h c", c=CH)
                    copy(FU[d][HD:P, :, :, CH:2 * CH].rearrange("p h r c -> p (h r) c"), as8(bank(d, 0)))
                    copy(ST[d][HD:P, :, :, :].rearrange("p h r c -> p (h r c)"), bank(d, 3)[0:CH, :])\
                        .then_inc(a_t2[d], 1)
                    for par, r in enumerate(ROWS):
                        ins = copy(FU[d][0:HD, :, par, 0:CH], AR[d][r, :, 1, :])
                    ins.then_inc(a_r[d], 1)

                def solved(d, i):
                    act.wait_ge(m_g[d], i + 1)
                    copy(GH[d][:].rearrange("p h c -> p (h c)"), bank(d, 2)[:]).then_inc(a_g[d], 1)

                def chunk(i, following):
                    for d in DIRS:
                        turned1(d, i)
                    for d in DIRS:
                        turned2(d, i)
                    if following is not None:
                        for d in DIRS:
                            tanh(d, following)
                        for d in DIRS:
                            exps(d, following)
                    for d in DIRS:
                        solved(d, i)

                for d in DIRS:
                    tanh(d, 0)
                for d in DIRS:
                    exps(d, 0)
                repeat(act, NCH, lambda i: chunk(i, i + 1), lambda i: chunk(i, None))

            @block.gpsimd
            def _(pool):
                ch = Chain(pool, pool_step)
                ka = g.vec[:, VEC["k_a"][0]:VEC["k_a"][0] + HP].unsqueeze(2).to_broadcast([P, HP, CH])
                tt = nc.gpsimd.tensor_tensor

                def factors(d, i):
                    at = bass.ds(col(d, i), CH)
                    last = CH - 1 if d == 0 else 0
                    end = WX[d][:, 0, :, last:last + 1].to_broadcast([P, HP, CH])
                    kk_, k = g.nkk[:, :, at], g.rkv[:, HP:2 * HP, at]
                    pool.wait_ge(m_c[d], i)
                    pool.wait_ge(a_r[d], i)
                    apart(pool, g, m_t2[d], i)
                    nc.gpsimd.tensor_copy(VC[d][:], g.rkv[:, 2 * HP:3 * HP, at]).then_inc(p_v[d], 1)
                    apart(pool, g, a_exp[d], i + 1)
                    ch.count(tt(AR[d][:, :, 0, :], kk_, WX[d][:, 1], ALU.mult))
                    ch.count(tt(AR[d][:, :, 1, :], g.rkv[:, 0:HP, at], WX[d][:, 0], ALU.mult))
                    ch.count(tt(BK[d][:, :, 0, :], kk_, SG[d][:, 1], ALU.mult))
                    ch.link(tt(OM[d][:], OM[d][:], ka, ALU.mult))
                    ch.count(tt(BK[d][:, :, 0, :], BK[d][:, :, 0, :], WX[d][:, 2], ALU.mult))
                    ch.link(tt(OM[d][:], OM[d][:], k, ALU.mult))
                    ch.count(tt(BH[d][:], BK[d][:, :, 0, :], end, ALU.mult))
                    ch.link(tt(OM[d][:], k, OM[d][:], ALU.subtract))
                    ch.link(tt(BK[d][:, :, 1, :], OM[d][:], WX[d][:, 2], ALU.mult))
                    tt(KH[d][:], BK[d][:, :, 1, :], end, ALU.mult).then_inc(v_prep[d], 1)

                for d in DIRS:
                    factors(d, 0)
                ch.begin()
                with pool.Fori(0, NCH - 1) as i:
                    ch.enter(i, 2 * 9)
                    for d in DIRS:
                        factors(d, i + 1)
                ch.leave(NCH - 1)

            @block.vector
            def _(dve):
                ch = Chain(dve, dve_step)
                ka = g.vec[:, VEC["k_a"][0]:VEC["k_a"][0] + HP].unsqueeze(2).to_broadcast([P, HP, CH])
                ident = lambda rows, n: g.c("ident_pair", rows=rows).unsqueeze(1).to_broadcast(
                    [rows.stop - rows.start, n, HD])
                b3 = lambda d, n: bank(d, n)[:].rearrange("p (h c) -> p h c", c=P)
                dve.wait_ge(g.s_const, 80)
                for d in DIRS:
                    ch.link(nc.vector.memset(ST[d][0:HD, :, :, :], 0.0))

                def end(d, rows):
                    last = CH - 1 if d == 0 else 0
                    return WX[d][rows, 0, :, last:last + 1].to_broadcast([rows.stop - rows.start, HP, CH])

                def sums(d, i):
                    dve.wait_ge(v_prep[d], i)
                    dve.wait_ge(a_th[d], i + 1)
                    flat = SG[d][:].rearrange("p n h c -> p n (h c)")
                    ts = nc.vector.tensor_scalar
                    ch.count(ts(cat(OM[d][:]), flat[:, 1, :], -0.5, 0.5, ALU.mult, ALU.add))
                    ch.link(ts(flat[:, 0, :], flat[:, 0, :], 0.5, 0.5, ALU.mult, ALU.add))
                    ch.count(ts(flat[:, 1, :], flat[:, 1, :], -0.5, -0.5, ALU.mult, ALU.add))
                    w = WX[d][:].rearrange("p n h c -> p n (h c)")
                    back = slice(None, None, -1) if d else slice(None)
                    ch.link(nc.vector.tensor_tensor_scan(w[:, 0, back], g.mk("reset"), flat[:, 0, back], 0.0,
                                                         ALU.mult, ALU.add))
                    nc.vector.tensor_tensor(w[:, 1, :], w[:, 0, :], flat[:, 0, :], ALU.subtract).then_inc(v_sum[d], 1)

                def diagonal(d, i):
                    dve.wait_ge(m_s[d], i)
                    for par, r in enumerate(ROWS):
                        ch.count(nc.vector.tensor_tensor(FU[d][0:HD, :, par, CH:2 * CH], ident(r, HP), end(d, r),
                                                         ALU.mult))

                def masked(d, i):
                    tt = nc.vector.tensor_tensor
                    dve.wait_ge(m_a[d], i + 1)
                    dve.wait_ge(m_g[d], i)
                    ch.count(tt(RB[d][:, :, 0:CH], b3(d, 1)[:, :, CH:2 * CH], mask("mask_y", d), ALU.mult))
                    ch.link(tt(NT[d][:], b3(d, 1)[:, :, 0:CH], mask("mask_nt", d), ALU.mult))
                    ch.link(tt(XX[d][:, :, 1, :], NT[d][:], mask("level_t", d), ALU.mult))
                    ch.count(tt(XX[d][:, :, 1, :], XX[d][:, :, 1, :], ident(slice(0, P), HP), ALU.add))
                    dve.wait_ge(m_b[d], i + 1)
                    ch.link(tt(XX[d][:, :, 0, :], b3(d, 2)[:, :, 0:CH], mask("level", d, 6), ALU.mult))
                    ch.link(tt(AM[d][:, :, CH:2 * CH], b3(d, 2)[:, :, CH:2 * CH], mask("mask_n", d), ALU.mult))
                    tt(XX[d][:, :, 0, :], XX[d][:, :, 0, :], ident(slice(0, P), HP), ALU.add).then_inc(v_b[d], 1)

                def masked_c(d, i):
                    dve.wait_ge(m_c[d], i + 1)
                    rows = slice(HD, P)
                    for par in range(2):
                        ins = nc.vector.tensor_tensor(
                            FU[d][rows, :, par, 0:CH],
                            bank(d, (3, 0)[par])[rows, 0:HP * CH].rearrange("p (h c) -> p h c", c=CH),
                            mask("mask_y", d, rows=rows), ALU.mult)
                        if par == 0:
                            ch.count(ins)
                    ins.then_inc(v_c[d], 1)

                def level_n(d, i, n):
                    dve.wait_ge(m_n[d], i * LEVELS + (n + 1))
                    nc.vector.tensor_tensor(T1[d][:], bank(d, 0)[:, 0:HP * CH].rearrange("p (h c) -> p h c", c=CH),
                                            mask("level", d, 6, n + 1), ALU.mult).then_inc(v_n[d], 1)

                def level_x(d, i, n):
                    dve.wait_ge(m_x[d], i * LEVELS + (n + 1))
                    src = bank(d, 1)[:].rearrange("p (h r c) -> p h r c", r=2, c=CH)
                    if n < LEVELS - 1:
                        ins = nc.vector.tensor_tensor(XX[d][:], src, XX[d][:], ALU.add)
                    else:
                        ins = nc.vector.tensor_tensor(XX[d][:, :, 0, :], src[:, :, 0, :], XX[d][:, :, 0, :], ALU.add)
                    ins.then_inc(v_x[d], 1)

                def summed(d, i):
                    dve.wait_ge(m_f[d], i + 1)
                    dve.wait_ge(a_r[d], i + 1)
                    for par in range(2):
                        ins = nc.vector.tensor_tensor(FU[d][:, :, par, :], b3(d, (0, 3)[par]), FU[d][:, :, par, :],
                                                      ALU.add)
                        if par == 0:
                            ch.count(ins)
                    ins.then_inc(v_f[d], 1)

                def out(d, i):
                    apart(dve, g, m_s[d], i + 1)
                    at = bass.ds(col(d, i), CH)
                    ch.link(nc.vector.tensor_tensor(
                        g.y[:, :, at], bank(d, 1)[:, 0:HP * CH].rearrange("p (h c) -> p h c", c=CH), g.y[:, :, at],
                        ALU.add))
                    base = CON["keep"][0] - N_CON + d * NCH
                    keep = g.masks[0:HD, bass.ds(i + base, 1)].to_broadcast([HD, 2 * HP * HD])
                    nc.vector.tensor_tensor(ST[d][0:HD, :, :, :].rearrange("p h r c -> p (h r c)"),
                                            bank(d, 2)[0:HD, :], keep, ALU.mult).then_inc(v_s[d], 1)

                def chunk(i, following):
                    for d in DIRS:
                        masked(d, i)
                        masked_c(d, i)
                    for n in range(LEVELS):
                        for d in DIRS:
                            level_n(d, i, n)
                            if n == 0:
                                diagonal(d, i)
                        for d in DIRS:
                            level_x(d, i, n)
                            if n == 1 and following is not None:
                                sums(d, following)
                    for d in DIRS:
                        summed(d, i)
                    for d in DIRS:
                        out(d, i)

                for d in DIRS:
                    sums(d, 0)
                ch.begin()

                def step(i):
                    ch.enter(i, 2 * (4 + 2 + 6 + 1 + 1 + 1))
                    chunk(i, i + 1)

                def last(i):
                    ch.leave(i)
                    chunk(i, None)

                repeat(dve, NCH, step, last)


def finish_branches(nc, a, g):
    N = HP * NB
    with ExitStack() as ctx:
        sb = lambda name, shape, dt=F32: ctx.enter_context(nc.sbuf_tensor(name, shape, dt))
        sem = nc.alloc_semaphore
        bonus = sb("bonus", [P, HP, T])
        sq = [sb(f"f_sq{j}", [P, BLK]) for j in range(2)]
        th = [sb(f"f_th{j}", [P, 2, BLK]) for j in range(2)]
        dev = [sb(f"f_dev{j}", [P, BLK]) for j in range(2)]
        inv = sb("f_inv", [P, NB, BLK])
        gup = sb("gup", [GLORA, HP, P])
        conv, y, v = g.conv, g.y, g.rkv[:, 2 * HP:3 * HP, :]
        loaded = sem("f_loaded")
        rate, rated, weighed = sem("f_rate"), sem("f_rated"), sem("f_weighed")
        mean, centred, squared, var, rooted, normed = (
            sem(f"f_{n}") for n in ("mean", "centred", "squared", "var", "rooted", "normed"))
        gated, done = sem("f_gated"), sem("f_done")
        c_mean, c_centred, c_squared, c_var, c_rooted, c_normed, c_done = (
            sem(f"fc_{n}") for n in ("mean", "centred", "squared", "var", "rooted", "normed", "done"))
        dve_step = sem("f_dve_step")
        pieces = [(hp, b) for hp in range(HP) for b in range(NB)]
        tok = lambda b: slice(b * BLK, (b + 1) * BLK)

        with nc.Block() as block:
            @block.sync
            def _(sp):
                sp.dma_start(g.sg[:], g.sg_dram).then_inc(loaded, 16)
                sp.dma_start(gup[:].rearrange("p h c -> p (h c)"), a["gate_up"]).then_inc(loaded, 16)
                sp.dma_start(conv[:], g.conv_dram).then_inc(loaded, 16)

            @block.tensor
            def _(pe):
                def mean_square(n):
                    pe.wait_ge(squared, n + 1)
                    if n >= 2:
                        pe.wait_ge(rooted, n - 1)
                    nc.tensor.matmul(g.bank[6 + n % 2][:], g.c("pair_sum"), sq[n % 2][:],
                                     start=True, stop=True).then_inc(var, 1)

                for n, (hp, b) in enumerate(pieces):
                    if n >= 2:
                        pe.wait_ge(rated, n - 1)
                    for d in range(2):
                        mm = nc.tensor.matmul(g.bank[2 * (n % 2) + d][:], g.upa[:, d, hp, :], g.la[:, tok(b)],
                                              start=True, stop=True)
                    mm.then_inc(rate, 1)
                    if n >= 2:
                        pe.wait_ge(centred, n - 1)
                    nc.tensor.matmul(g.bank[4 + n % 2][:], g.c("pair_sum"), y[:, hp, tok(b)],
                                     start=True, stop=True).then_inc(mean, 1)
                    if n >= 1:
                        mean_square(n - 1)
                mean_square(N - 1)
                pe.wait_ge(loaded, 48)
                pe.wait_ge(rated, N)
                for n, (hp, b) in enumerate(pieces):
                    pe.wait_ge(weighed, n + 1)
                    if n >= 2:
                        pe.wait_ge(done, n - 1)
                    nc.tensor.matmul(g.bank[2 * (n % 2)][:], g.c("pair_sum"), bonus[:, hp, tok(b)],
                                     start=True, stop=True)
                    nc.tensor.matmul(g.bank[2 * (n % 2) + 1][:], gup[:, hp, :], g.sg[:, tok(b)],
                                     start=True, stop=True).then_inc(gated, 1)
                pe.wait_ge(centred, N)
                pe.wait_ge(rooted, N)
                for b in range(NB):
                    if b >= 2:
                        pe.wait_ge(c_centred, CT * (b - 1))
                    for i in range(CT):
                        mm = nc.tensor.matmul(g.bank[4 + b % 2][:], g.c("ones"), conv[:, i, tok(b)],
                                              start=(i == 0), stop=(i == CT - 1))
                    mm.then_inc(c_mean, 1)
                for b in range(NB):
                    if b >= 2:
                        pe.wait_ge(c_rooted, b - 1)
                    for i in range(CT):
                        pe.wait_ge(c_squared, CT * b + i + 1)
                        nc.tensor.matmul(g.bank[6 + b % 2][:], g.c("ones"), sq[i % 2][:],
                                         start=(i == 0), stop=(i == CT - 1)).then_inc(c_var, 1)

            @block.scalar
            def _(act):
                def deviation_c(b):
                    act.wait_ge(c_var, CT * (b + 1))
                    nc.scalar.activation(inv[:, b, :], g.bank[6 + b % 2][:], ACT.Sqrt,
                                         bias=g.c("eps", 2, 1), scale=1.0 / CC).then_inc(c_rooted, 1)

                def deviation(n):
                    act.wait_ge(var, n + 1)
                    if n >= 2:
                        act.wait_ge(normed, n - 1)
                    nc.scalar.activation(dev[n % 2][:], g.bank[6 + n % 2][:], ACT.Sqrt,
                                         bias=g.c("eps", 1, 1), scale=1.0 / HD).then_inc(rooted, 1)

                for n, (hp, b) in enumerate(pieces):
                    act.wait_ge(rate, n + 1)
                    if n >= 2:
                        act.wait_ge(weighed, n - 1)
                    for d in range(2):
                        ins = nc.scalar.activation(th[n % 2][:, d, :], g.bank[2 * (n % 2) + d][:], ACT.Tanh,
                                                   scale=0.5)
                    ins.then_inc(rated, 1)
                    act.wait_ge(centred, n + 1)
                    if n >= 2:
                        act.wait_ge(var, n - 1)
                    nc.scalar.activation(sq[n % 2][:], y[:, hp, tok(b)], ACT.Square).then_inc(squared, 1)
                    if n >= 1:
                        deviation(n - 1)
                deviation(N - 1)
                for b in range(NB):
                    for i in range(CT):
                        k = CT * b + i
                        act.wait_ge(c_centred, k + 1)
                        if k >= 2:
                            act.wait_ge(c_var, k - 1)
                        nc.scalar.activation(sq[i % 2][:], conv[:, i, tok(b)], ACT.Square).then_inc(c_squared, 1)
                    if b >= 1:
                        deviation_c(b - 1)
                deviation_c(NB - 1)
                for b in range(NB):
                    for i in range(CT):
                        act.wait_ge(c_normed, CT * b + i + 1)
                        nc.scalar.activation(conv[:, i, tok(b)], conv[:, i, tok(b)], ACT.Silu,
                                             bias=g.v("conv_ln_b", i), scale=g.v("conv_ln_w", i)).then_inc(c_done, 1)

            @block.vector
            def _(dve):
                ch = Chain(dve, dve_step)
                tt, ts, stt = nc.vector.tensor_tensor, nc.vector.tensor_scalar, nc.vector.scalar_tensor_tensor

                def normalise(n):
                    hp, b = pieces[n]
                    yt = y[:, hp, tok(b)]
                    dve.wait_ge(rooted, n + 1)
                    ch.link(nc.vector.reciprocal(dev[n % 2][:], dev[n % 2][:]))
                    stt(yt, yt, g.v("lnx_w", hp), dev[n % 2][:], ALU.mult, ALU.mult).then_inc(normed, 1)

                for n, (hp, b) in enumerate(pieces):
                    yt = y[:, hp, tok(b)]
                    dve.wait_ge(mean, n + 1)
                    stt(yt, g.bank[4 + n % 2][:], -1.0 / HD, yt, ALU.mult, ALU.add).then_inc(centred, 1)
                    w = bonus[:, hp, tok(b)]
                    dve.wait_ge(rated, n + 1)
                    ch.link(tt(w, th[n % 2][:, 0, :], th[n % 2][:, 1, :], ALU.add))
                    ch.link(ts(w, w, 0.5, -1.0, ALU.mult, ALU.add))
                    ch.link(ts(w, w, g.v("k_a", hp), 2.0, ALU.mult, ALU.add))
                    ch.link(tt(w, w, g.rkv[:, HP + hp, tok(b)], ALU.mult))
                    stt(w, w, g.v("r_k", hp), g.rkv[:, hp, tok(b)], ALU.mult, ALU.mult).then_inc(weighed, 1)
                    if n >= 1:
                        normalise(n - 1)
                normalise(N - 1)
                dve.wait_ge(weighed, N)
                dve.wait_ge(normed, N)
                for n, (hp, b) in enumerate(pieces):
                    yt, w = y[:, hp, tok(b)], bonus[:, hp, tok(b)]
                    dve.wait_ge(gated, n + 1)
                    ch.link(tt(w, g.bank[2 * (n % 2)][:], v[:, hp, tok(b)], ALU.mult))
                    ch.link(stt(yt, yt, g.v("lnx_b", hp), w, ALU.add, ALU.add))
                    tt(yt, g.bank[2 * (n % 2) + 1][:], yt, ALU.mult).then_inc(done, 1)
                for b in range(NB):
                    dve.wait_ge(c_mean, b + 1)
                    for i in range(CT):
                        ct = conv[:, i, tok(b)]
                        stt(ct, g.bank[4 + b % 2][:], -1.0 / CC, ct, ALU.mult, ALU.add).then_inc(c_centred, 1)
                for b in range(NB):
                    dve.wait_ge(c_rooted, b + 1)
                    ch.link(nc.vector.reciprocal(inv[:, b, :], inv[:, b, :]))
                    for i in range(CT):
                        ct = conv[:, i, tok(b)]
                        tt(ct, ct, inv[:, b, :], ALU.mult).then_inc(c_normed, 1)


def merge(nc, a, g):
    with ExitStack() as ctx:
        sb = lambda name, shape, dt=F32: ctx.enter_context(nc.sbuf_tensor(name, shape, dt))
        sem = nc.alloc_semaphore
        w = [sb(f"m_w{j}", [P, 2 * HP, P]) for j in range(2)]
        ga = [sb(f"m_ga{j}", [P, T]) for j in range(2)]
        gb = [sb(f"m_gb{j}", [P, T]) for j in range(2)]
        loaded = [sem(f"m_loaded{j}") for j in range(2)]
        multiplied, mixed = [sem(f"m_multiplied{j}") for j in range(2)], [sem(f"m_mixed{j}") for j in range(2)]
        stored = [sem(f"m_stored{j}") for j in range(2)]
        dve_step = sem("m_dve_step")
        gates = g.gates.rearrange("(s k p) t -> s k p t", s=2, p=P)
        with nc.Block() as block:
            @block.sync
            def _(sp):
                def load(i):
                    for j in range(2):
                        apart(sp, g, multiplied[j], i * NB)
                        sp.wait_ge(stored[j], i * 16)
                        sp.dma_start(w[j][:].rearrange("p k c -> p (k c)"), a["w_o"][2 * i + j, :, :])\
                          .then_inc(loaded[j], 16)
                        sp.dma_start(ga[j][:], gates[0, 2 * i + j, :, :]).then_inc(loaded[j], 16)
                        sp.dma_start(gb[j][:], gates[1, 2 * i + j, :, :]).then_inc(loaded[j], 16)

                repeat(sp, KD // 2, load)

            @block.tensor
            def _(pe):
                def tiles(i):
                    for j in range(2):
                        pe.wait_ge(loaded[j], i * 48 + 48)
                        for b in range(NB):
                            n = NB * j + b
                            s = n % 3
                            if n >= 3:
                                pe.wait_ge(mixed[0], i * NB + (n - 3 + 1))
                            else:
                                pe.wait_ge(mixed[1], i * NB)
                            for half, src in ((0, g.y), (1, g.conv)):
                                for k in range(HP):
                                    mm = nc.tensor.matmul(g.bank[2 * s + half][:], w[j][:, half * HP + k, :],
                                                          src[:, k, b * BLK:(b + 1) * BLK],
                                                          start=(k == 0), stop=(k == HP - 1))
                            mm.then_inc(multiplied[j], 1)

                repeat(pe, KD // 2, tiles)

            @block.vector
            def _(dve):
                ch = Chain(dve, dve_step)
                ch.begin()
                with dve.Fori(0, KD // 2) as i:
                    ch.enter(i, 4 * NB)
                    for j in range(2):
                        for b in range(NB):
                            s = (NB * j + b) % 3
                            dve.wait_ge(multiplied[j], i * NB + (b + 1))
                            pa, pb = ga[j][:, b * BLK:(b + 1) * BLK], gb[j][:, b * BLK:(b + 1) * BLK]
                            ch.count(nc.vector.tensor_tensor(pa, g.bank[2 * s][:], pa, ALU.mult))
                            ch.link(nc.vector.tensor_tensor(pb, g.bank[2 * s + 1][:], pb, ALU.mult))
                            nc.vector.tensor_tensor(pa, pa, pb, ALU.add).then_inc(mixed[j], 1)
                ch.leave(KD // 2)

            @block.scalar
            def _(act):
                with act.Fori(0, KD // 2) as i:
                    for j in range(2):
                        act.wait_ge(mixed[j], i * NB + NB)
                        act.dma_start(g.mix[2 * i + j, :, :], ga[j][:]).then_inc(stored[j], 16)
                for j in range(2):
                    act.wait_ge(stored[j], 16 * KD // 2)


def add_and_route(nc, a, g):
    NT = T // P
    with ExitStack() as ctx:
        sb = lambda name, shape, dt=F32: ctx.enter_context(nc.sbuf_tensor(name, shape, dt))
        sem = nc.alloc_semaphore
        m = sb("r_m", [P, KD, T])
        w = sb("r_w", [P, KD, D])
        x = [sb(f"r_x{j}", [P, D]) for j in range(2)]
        h = [sb(f"r_h{j}", [P, D]) for j in range(2)]
        ht = [sb(f"r_ht{j}", [P, KD, P]) for j in range(2)]
        norm = sb("r_norm", [P, D])
        junk = sb("r_junk", [P, D])
        rw = sb("r_rw", [P, KD, E])
        rb = sb("r_rb", [1, E])
        small = [sb(f"r_small{j}", [P, 8]) for j in range(2)]
        aff = [sb(f"r_aff{j}", [P, E]) for j in range(2)]
        score = sb("r_score", [48, T_SAMPLE])
        top = sb("r_top", [48, CAP[1]])
        place = sb("r_place", [48, CAP[1]], U32)
        placef = sb("r_placef", [48, CAP[1]])
        w_in, c_in = sem("r_w_in"), sem("r_c_in")
        m_in = [sem(f"r_m_in{k}") for k in range(KD)]
        x_in = [sem(f"r_x_in{j}") for j in range(2)]
        stored = [sem(f"r_stored{j}") for j in range(2)]
        mixed, added, squared, rooted, h_done, turned, copied, scored, exped, weighed, aff_t, filled = (
            sem(f"r_{n}") for n in ("mixed", "added", "squared", "rooted", "h_done", "turned", "copied",
                                    "scored", "exped", "weighed", "aff_t", "filled"))
        dve_step, picked, picked_t, scored2 = sem("r_dve_step"), sem("r_picked"), sem("r_picked_t"), sem("r_maximum")
        with nc.Block() as block:
            @block.sync
            def _(sp):
                sp.dma_start(w[:], a["w_out"]).then_inc(w_in, 16)
                for k in range(KD):
                    sp.dma_start(m[:, k, :], g.mix[k, :, :]).then_inc(m_in[k], 16)
                for t in range(NT):
                    if t >= 2:
                        sp.wait_ge(stored[t % 2], 32 * (t // 2))
                    sp.dma_start(x[t % 2][:], a["x"][t * P:(t + 1) * P, :]).then_inc(x_in[t % 2], 16)

            @block.gpsimd
            def _(pool):
                pool.dma_start(norm[:], a["norms"][0:1, :].to_broadcast([P, D])).then_inc(c_in, 16)
                pool.dma_start(rw[:], a["router_w"]).then_inc(c_in, 16)
                pool.dma_start(rb[:], a["router_b"]).then_inc(c_in, 16)
                for t in range(NT):
                    pool.wait_ge(added, 2 * (t + 1))
                    pool.dma_start(g.xacc[t * P:(t + 1) * P, :], x[t % 2][:]).then_inc(stored[t % 2], 16)
                    pool.wait_ge(h_done, t + 1)
                    pool.dma_start(g.h2[t * P:(t + 1) * P, :], h[t % 2][:]).then_inc(stored[t % 2], 16)
                for j in range(2):
                    pool.wait_ge(stored[j], 32 * NT // 2)

            @block.tensor
            def _(pe):
                pe.wait_ge(w_in, 16)
                pe.wait_ge(c_in, 48)
                for k in range(KD):
                    pe.wait_ge(m_in[k], 16)

                def project_out(t):
                    for half in range(2):
                        if t >= 2:
                            pe.wait_ge(added, 2 * (t - 1))
                        for k in range(KD):
                            mm = nc.tensor.matmul(g.bank[2 * (t % 2) + half][:], m[:, k, t * P:(t + 1) * P],
                                                  w[:, k, half * BLK:(half + 1) * BLK],
                                                  start=(k == 0), stop=(k == KD - 1))
                        mm.then_inc(mixed, 1)

                def route(t):
                    pe.wait_ge(h_done, t + 1)
                    if t >= 1:
                        pe.wait_ge(copied, 2 * t)
                    for k in range(KD):
                        mm = nc.tensor.transpose(g.bank[4 + k // 4][:, (k % 4) * P:(k % 4 + 1) * P],
                                                 h[t % 2][:, k * P:(k + 1) * P], g.c("ident"))
                        if k % 4 == 3:
                            mm.then_inc(turned, 1)
                    pe.wait_ge(copied, 2 * (t + 1))
                    if t >= 1:
                        pe.wait_ge(weighed, t)
                    for k in range(KD):
                        nc.tensor.matmul(g.bank[6][:, 0:E], ht[t % 2][:, k, :], rw[:, k, :],
                                         start=(k == 0), stop=False)
                    nc.tensor.matmul(g.bank[6][:, 0:E], g.c("ones", rows=slice(0, 1)), rb[:],
                                     start=False, stop=True).then_inc(scored, 1)

                def turn_scores(t):
                    pe.wait_ge(weighed, t + 1)
                    if t >= 1:
                        pe.wait_ge(filled, t)
                    nc.tensor.transpose(g.bank[7][0:E, 0:P], aff[t % 2][:], g.c("ident")).then_inc(aff_t, 1)

                for t in range(NT + 2):
                    if t < NT:
                        project_out(t)
                    if 1 <= t <= NT:
                        route(t - 1)
                    if t >= 2:
                        turn_scores(t - 2)
                pe.wait_ge(picked, 1)
                nc.tensor.transpose(g.bank[4][0:P, 0:48], top[:], g.c("ident", n=48, rows=slice(0, 48)))
                nc.tensor.transpose(g.bank[5][0:P, 0:48], placef[:], g.c("ident", n=48, rows=slice(0, 48)))\
                  .then_inc(picked_t, 1)

            @block.scalar
            def _(act):
                def route(t):
                    for half in range(2):
                        act.wait_ge(turned, 2 * t + half + 1)
                        nc.scalar.activation(ht[t % 2][:, 4 * half:4 * half + 4, :].rearrange("p k c -> p (k c)"),
                                             g.bank[4 + half][:], ACT.Copy).then_inc(copied, 1)
                    act.wait_ge(scored2, t + 1)
                    nc.scalar.activation(aff[t % 2][:], g.bank[6][:, 0:E], ACT.Exp, bias=small[t % 2][:, 4:5],
                                         accum_out=small[t % 2][:, 5:6]).then_inc(exped, 1)

                for t in range(NT):
                    act.wait_ge(added, 2 * (t + 1))
                    nc.scalar.activation(junk[:], x[t % 2][:], ACT.Square,
                                         accum_out=small[t % 2][:, 0:1]).then_inc(squared, 1)
                    act.wait_ge(squared, t + 1)
                    nc.scalar.activation(small[t % 2][:, 1:2], small[t % 2][:, 0:1], ACT.Sqrt,
                                         bias=g.c("eps", 0, 1), scale=1.0 / D).then_inc(rooted, 1)
                    if t >= 1:
                        route(t - 1)
                route(NT - 1)

            @block.vector
            def _(dve):
                ch = Chain(dve, dve_step)
                ch.link(nc.vector.memset(score[:], -1.0))
                dve.wait_ge(c_in, 48)

                def finish(t):
                    s = small[t % 2]
                    dve.wait_ge(scored, t + 1)
                    nc.vector.tensor_reduce(s[:, 4:5], g.bank[6][:, 0:E], AXIS.X, ALU.max, negate=True)\
                      .then_inc(scored2, 1)
                    dve.wait_ge(exped, t + 1)
                    ch.link(nc.vector.reciprocal(s[:, 6:7], s[:, 5:6]))
                    nc.vector.tensor_scalar(aff[t % 2][:], aff[t % 2][:], s[:, 6:7], None, ALU.mult)\
                      .then_inc(weighed, 1)

                def fill(t):
                    dve.wait_ge(aff_t, t + 1)
                    row, at = (0, t * P) if t * P < T_PROMPT else (32, t * P - T_PROMPT)
                    nc.vector.tensor_copy(score[row:row + E, at:at + P], g.bank[7][0:E, 0:P]).then_inc(filled, 1)

                for t in range(NT + 2):
                    if t < NT:
                        s = small[t % 2]
                        dve.wait_ge(x_in[t % 2], 16 * (t // 2 + 1))
                        for half in range(2):
                            c = slice(half * BLK, (half + 1) * BLK)
                            dve.wait_ge(mixed, 2 * t + half + 1)
                            nc.vector.tensor_tensor(x[t % 2][:, c], g.bank[2 * (t % 2) + half][:], x[t % 2][:, c],
                                                    ALU.add).then_inc(added, 1)
                        dve.wait_ge(rooted, t + 1)
                        ch.link(nc.vector.reciprocal(s[:, 2:3], s[:, 1:2]))
                        if t >= 2:
                            dve.wait_ge(stored[t % 2], 32 * (t // 2))
                        nc.vector.scalar_tensor_tensor(h[t % 2][:], x[t % 2][:], s[:, 2:3], norm[:],
                                                       ALU.mult, ALU.mult).then_inc(h_done, 1)
                    if 1 <= t <= NT:
                        finish(t - 1)
                    if t >= 2:
                        fill(t - 2)
                dve.wait_ge(filled, NT)
                for n in range(CAP[1] // 8):
                    c = slice(8 * n, 8 * n + 8)
                    ch.link(nc.vector.max(top[:, c], score[:]))
                    ch.link(nc.vector.max_index(place[:, c], top[:, c], score[:]))
                    ch.link(nc.vector.match_replace(score[:], top[:, c], score[:], -1.0))
                nc.vector.tensor_copy(placef[:], place[:]).then_inc(picked, 1)
                dve.wait_ge(picked_t, 1)
                for n in range(2):
                    rows = slice(0, CAP[n])
                    nc.vector.tensor_copy(g.gate[rows, n, :], g.bank[4][rows, 32 * n:32 * n + E])
                    ch.link(nc.vector.tensor_scalar(g.index[rows, n, :], g.bank[5][rows, 32 * n:32 * n + E],
                                                    float(T_PROMPT * n), None, ALU.add))


def experts(nc, a, g):
    SLOTS = CAP[0] + CAP[1]
    UNITS, RING = 12, 6
    with ExitStack() as ctx:
        sb = lambda name, shape, dt=F32: ctx.enter_context(nc.sbuf_tensor(name, shape, dt))
        sem = nc.alloc_semaphore
        w = [sb(f"e_w{n}", [P, 2048]) for n in range(RING)]
        w_high = [sb(f"e_w_high{n}", [P, 2048], F32R) for n in range(RING)]
        w_low = [sb(f"e_w_low{n}", [P, 2048], F32R) for n in range(RING)]
        xe = [sb(f"e_x{n}", [CAP[n], D]) for n in range(2)]
        xt = sb("e_xt", [P, KD, 2, SLOTS], F32R)
        hid_high, hid_low = sb("e_hid_high", [P, KD, SLOTS], F32R), sb("e_hid_low", [P, KD, SLOTS], F32R)
        hid = [sb(f"e_hid{j}", [P, SLOTS]) for j in range(2)]
        sums = [sb(f"e_sums{j}", [P, 2, SLOTS]) for j in range(2)]
        act_ = [sb(f"e_act{j}", [P, SLOTS]) for j in range(2)]
        ye = [sb(f"e_y{n}", [CAP[n], D]) for n in range(2)]
        row = [sb(f"e_row{n}", [CAP[n], 1], U32) for n in range(2)]
        put = [sb(f"e_put{n}", [CAP[n], 1], U32) for n in range(2)]
        wt = [sb(f"e_wt{n}", [CAP[n], 1]) for n in range(2)]
        w_in = [sem(f"e_w_in{n}") for n in range(RING)]
        rows_ready, fetched, turned, x_high, x_split = (
            sem(f"e_{n}") for n in ("rows_ready", "fetched", "turned", "x_high", "x_split"))
        w_high_done, w_split = sem("e_w_high_done"), sem("e_w_split")
        up_done, copied, summed, silu_done, hid_done, hid_high_done, hid_split = (
            sem(f"e_{n}") for n in ("up_done", "copied", "summed", "silu_done", "hid_done", "hid_high_done", "hid_split"))
        down_done, scaled, added, weights_ready = (
            sem(f"e_{n}") for n in ("down_done", "scaled", "added", "weights_ready"))
        FT = FF // P

        def upcoming(e, n):
            return (e, n) if n < UNITS else (e + 1, n - UNITS)

        with nc.Block() as block:
            @block.sync
            def _(sp):
                def load(e):
                    for n in range(UNITS):
                        if not isinstance(e, int) or n >= RING:
                            apart(sp, g, w_split, e * UNITS + (n - RING + 1))
                        sp.dma_start(w[n % RING][:], a["ew"][e, n, :, :]).then_inc(w_in[n % RING], 16)

                repeat(sp, E, load)

            @block.gpsimd
            def _(pool):
                def fetch(e):
                    apart(pool, g, rows_ready, e + 1)
                    apart(pool, g, turned, 4 * e)
                    for n in range(2):
                        pool.indirect_dma_start(xe[n][:], None, g.h2, bass.IndirectOffsetOnAxis(ap=row[n][:], axis=0))\
                          .then_inc(fetched, 16)

                def add(e):
                    apart(pool, g, scaled, 4 * e + 4)
                    for n in range(2):
                        pool.indirect_dma_start(g.xacc, bass.IndirectOffsetOnAxis(ap=put[n][:], axis=0), ye[n][:],
                                                None, compute_op=ALU.add).then_inc(added, 16)
                    apart(pool, g, added, e * 32 + 32)

                fetch(0)
                with pool.Fori(0, E - 1) as e:
                    fetch(e + 1)
                    add(e)
                add(E - 1)

            @block.tensor
            def _(pe):
                def product(out, left, right, first, last):
                    nc.tensor.matmul(out, left[0], right[0], start=first, stop=False)
                    nc.tensor.matmul(out, left[0], right[1], start=False, stop=False)
                    return nc.tensor.matmul(out, left[1], right[0], start=False, stop=last)

                def turn(e, q):
                    if q == 0:
                        apart(pe, g, fetched, e * 32 + 32)
                    if not isinstance(e, int) or e > 0:
                        apart(pe, g, summed, e * FT + (q // 2 - 1))
                    for k in (2 * q, 2 * q + 1):
                        at = (k % 2) * SLOTS
                        nc.tensor.transpose(g.bank[4 + q][:, at:at + CAP[1]], xe[1][:, k * P:(k + 1) * P],
                                            g.c("ident"))
                        mm = nc.tensor.transpose(g.bank[4 + q][:, at + CAP[1]:at + SLOTS],
                                                 xe[0][:, k * P:(k + 1) * P],
                                                 g.c("ident", n=CAP[0], rows=slice(0, CAP[0])))
                    mm.then_inc(turned, 1)

                def feed(e):
                    for f in range(FT):
                        u = 2 * (f // 2)
                        if f % 2 == 0:
                            apart(pe, g, w_split, e * UNITS + (u + 2))
                        if f < 2:
                            apart(pe, g, summed, FT * e)
                        else:
                            apart(pe, g, summed, e * FT + (f - 1))
                        if f == 0:
                            apart(pe, g, x_split, e * 4 + 4)
                        for side in range(2):
                            n = (u + side) % RING
                            c = lambda t, k: t[:, k * 2 * P + (f % 2) * P:k * 2 * P + (f % 2 + 1) * P]
                            out = g.bank[4 + 2 * (f % 2) + side]
                            for k in range(KD):
                                wide = (out[:, 0:2 * SLOTS], c(w_high[n], k),
                                        xt[:, k, :, :].rearrange("p s c -> p (s c)"))
                                narrow = (out[:, 0:SLOTS], c(w_low[n], k), xt[:, k, 0, :])
                                if k < KD - 1:
                                    nc.tensor.matmul(*wide, start=(k == 0), stop=False)
                                    nc.tensor.matmul(*narrow, start=False, stop=False)
                                else:
                                    nc.tensor.matmul(*narrow, start=False, stop=False)
                                    mm = nc.tensor.matmul(*wide, start=False, stop=True)
                        mm.then_inc(up_done, 1)

                def down(e, f):
                    if f == 0:
                        apart(pe, g, scaled, e * 4)
                    if f % 2 == 0:
                        apart(pe, g, w_split, e * UNITS + (8 + f // 2 + 1))
                    apart(pe, g, hid_split, e * FT + (f + 1))
                    u = (8 + f // 2) % RING
                    for n, lo in ((1, 0), (0, CAP[1])):
                        c = slice(lo, lo + CAP[n])
                        for half in range(2):
                            at = slice((f % 2) * D + half * BLK, (f % 2) * D + (half + 1) * BLK)
                            mm = product(g.bank[2 * n + half][0:CAP[n], :], (hid_high[:, f, c], hid_low[:, f, c]),
                                         (w_high[u][:, at], w_low[u][:, at]), f == 0, f == FT - 1)
                    mm.then_inc(down_done, 1)

                for q in range(4):
                    turn(0, q)

                def expert(e):
                    feed(e)
                    turn(e + 1, 0)
                    turn(e + 1, 1)
                    for f in range(FT):
                        down(e, f)
                        if f in (1, 2):
                            turn(e + 1, f + 1)

                def last(e):
                    feed(e)
                    for f in range(FT):
                        down(e, f)

                repeat(pe, E, expert, last)

            @block.scalar
            def _(act):
                def weights_high(e, n):
                    act.wait_ge(w_in[n % RING], e * 32 + (16 * (n // RING) + 16))
                    if n >= RING:
                        act.wait_ge(up_done, e * FT + 2 * ((n - RING) // 2) + 2)
                    elif n < 2:
                        act.wait_ge(up_done, e * FT)
                    elif not isinstance(e, int) or e > 0:
                        act.wait_ge(down_done, e * FT + (2 * n - 10))
                    nc.scalar.activation(w_high[n % RING][:], w[n % RING][:], ACT.Copy).then_inc(w_high_done, 1)

                def hidden_high(e, f):
                    act.wait_ge(hid_done, e * FT + (f + 1))
                    nc.scalar.activation(hid_high[:, f, :], hid[f % 2][:], ACT.Copy).then_inc(hid_high_done, 1)

                def tokens_high(e, q):
                    act.wait_ge(turned, e * 4 + (q + 1))
                    nc.scalar.activation(xt[:, 2 * q:2 * q + 2, 0, :],
                                         g.bank[4 + q][:, 0:2 * SLOTS].rearrange("p (k c) -> p k c", k=2),
                                         ACT.Copy).then_inc(x_high, 1)

                def expert(e, more=True):
                    for f in range(FT):
                        act.wait_ge(up_done, e * FT + (f + 1))
                        act.wait_ge(hid_done, e * FT + (f - 1 if f >= 2 else 0))
                        for side in range(2):
                            nc.scalar.activation(sums[f % 2][:, side, :],
                                                 g.bank[4 + 2 * (f % 2) + side][:, SLOTS:2 * SLOTS], ACT.Copy)\
                              .then_inc(copied, 1)
                        if f == 0:
                            act.wait_ge(down_done, e * FT)
                        else:
                            hidden_high(e, f - 1)
                        act.wait_ge(summed, e * FT + (f + 1))
                        nc.scalar.activation(act_[f % 2][:], sums[f % 2][:, 0, :], ACT.Silu).then_inc(silu_done, 1)
                        if f >= 1 and (more or f + 5 < UNITS):
                            weights_high(*upcoming(e, f + 5))
                    hidden_high(e, FT - 1)
                    if more:
                        tokens_high(e + 1, 0)
                        tokens_high(e + 1, 1)
                        weights_high(e + 1, 1)
                        tokens_high(e + 1, 2)
                        tokens_high(e + 1, 3)
                        for n in range(2, RING):
                            weights_high(e + 1, n)

                for n in range(2):
                    weights_high(0, n)
                for q in range(4):
                    tokens_high(0, q)
                for n in range(2, RING):
                    weights_high(0, n)
                repeat(act, E, expert, lambda e: expert(e, False))

            @block.vector
            def _(dve):
                tt = nc.vector.tensor_tensor

                def rows(e):
                    dve.wait_ge(fetched, e * 32)
                    for n in range(2):
                        ins = nc.vector.tensor_copy(row[n][:], g.index[0:CAP[n], n, bass.ds(e, 1)])
                    ins.then_inc(rows_ready, 1)

                def weights_low(e, n):
                    dve.wait_ge(w_high_done, e * UNITS + (n + 1))
                    tt(w_low[n % RING][:], w[n % RING][:], w_high[n % RING][:].bitcast(F32), ALU.subtract)\
                      .then_inc(w_split, 1)

                def hidden_low(e, f):
                    dve.wait_ge(hid_high_done, e * FT + (f + 1))
                    tt(hid_low[:, f, :], hid[f % 2][:], hid_high[:, f, :].bitcast(F32), ALU.subtract)\
                      .then_inc(hid_split, 1)

                def tokens_low(e, q):
                    dve.wait_ge(x_high, e * 4 + (q + 1))
                    part = lambda low: xt[:, 2 * q:2 * q + 2, low, :]
                    tt(part(1), g.bank[4 + q][:, 0:2 * SLOTS].rearrange("p (k c) -> p k c", k=2),
                       part(0).bitcast(F32), ALU.subtract)\
                      .then_inc(x_split, 1)

                def scale(e):
                    dve.wait_ge(added, e * 32)
                    for n in range(2):
                        nc.vector.tensor_copy(put[n][:], g.index[0:CAP[n], n, bass.ds(e, 1)])
                        ins = nc.vector.tensor_copy(wt[n][:], g.gate[0:CAP[n], n, bass.ds(e, 1)])
                    ins.then_inc(weights_ready, 1)
                    dve.wait_ge(weights_ready, e + 1)
                    dve.wait_ge(down_done, e * FT + FT)
                    for n in range(2):
                        for half in range(2):
                            nc.vector.tensor_scalar(ye[n][:, half * BLK:(half + 1) * BLK],
                                                    g.bank[2 * n + half][0:CAP[n], :], wt[n][:], None, ALU.mult)\
                              .then_inc(scaled, 1)

                def expert(e, more=True):
                    if more:
                        rows(e + 1)
                    for f in range(FT):
                        for side in range(2):
                            dve.wait_ge(copied, e * 2 * FT + (2 * f + side + 1))
                            half = sums[f % 2][:, side, :]
                            ins = tt(half, g.bank[4 + 2 * (f % 2) + side][:, 0:SLOTS], half, ALU.add)
                        ins.then_inc(summed, 1)
                        if f >= 1:
                            hidden_low(e, f - 1)
                        if f >= 2:
                            weights_low(e, f + 4)
                        dve.wait_ge(silu_done, e * FT + (f + 1))
                        dve.wait_ge(summed, e * FT + (f + 1))
                        dve.wait_ge(hid_split, e * FT + (f - 1 if f >= 2 else 0))
                        tt(hid[f % 2][:], sums[f % 2][:, 1, :], act_[f % 2][:], ALU.mult).then_inc(hid_done, 1)
                    hidden_low(e, FT - 1)
                    if more:
                        tokens_low(e + 1, 0)
                        tokens_low(e + 1, 1)
                        weights_low(e + 1, 0)
                        weights_low(e + 1, 1)
                        tokens_low(e + 1, 2)
                        tokens_low(e + 1, 3)
                        for n in range(2, RING):
                            weights_low(e + 1, n)
                    scale(e)

                rows(0)
                for n in range(2):
                    weights_low(0, n)
                for q in range(4):
                    tokens_low(0, q)
                for n in range(2, RING):
                    weights_low(0, n)
                repeat(dve, E, expert, lambda e: expert(e, False))


def final_norm(nc, a, g):
    NT = T // P
    with ExitStack() as ctx:
        sb = lambda name, shape, dt=F32: ctx.enter_context(nc.sbuf_tensor(name, shape, dt))
        sem = nc.alloc_semaphore
        x = [sb(f"n_x{j}", [P, D]) for j in range(4)]
        junk = sb("n_junk", [P, D])
        norm = sb("n_norm", [P, D])
        small = sb("n_small", [P, NT, 4])
        c_in, dve_step = sem("n_c_in"), sem("n_dve_step")
        x_in, stored = [sem(f"n_x_in{j}") for j in range(4)], [sem(f"n_stored{j}") for j in range(4)]
        squared, rooted, normed = sem("n_squared"), sem("n_rooted"), sem("n_normed")
        with nc.Block() as block:
            @block.sync
            def _(sp):
                sp.dma_start(norm[:], a["norms"][1:2, :].to_broadcast([P, D])).then_inc(c_in, 16)
                for t in range(NT):
                    if t >= 4:
                        sp.wait_ge(stored[t % 4], 16 * (t // 4))
                    sp.dma_start(x[t % 4][:], g.xacc[t * P:(t + 1) * P, :]).then_inc(x_in[t % 4], 16)

            @block.scalar
            def _(act):
                for t in range(NT):
                    act.wait_ge(x_in[t % 4], 16 * (t // 4 + 1))
                    nc.scalar.activation(junk[:], x[t % 4][:], ACT.Square, accum_out=small[:, t, 0:1])\
                      .then_inc(squared, 1)
                    act.wait_ge(squared, t + 1)
                    nc.scalar.activation(small[:, t, 1:2], small[:, t, 0:1], ACT.Sqrt, bias=g.c("eps", 0, 1),
                                         scale=1.0 / D).then_inc(rooted, 1)

            @block.vector
            def _(dve):
                ch = Chain(dve, dve_step)
                dve.wait_ge(c_in, 16)
                for t in range(NT):
                    dve.wait_ge(rooted, t + 1)
                    ch.link(nc.vector.reciprocal(small[:, t, 2:3], small[:, t, 1:2]))
                    nc.vector.scalar_tensor_tensor(x[t % 4][:], x[t % 4][:], small[:, t, 2:3], norm[:],
                                                   ALU.mult, ALU.mult).then_inc(normed, 1)

            @block.gpsimd
            def _(pool):
                for t in range(NT):
                    pool.wait_ge(normed, t + 1)
                    pool.dma_start(a["out"][t * P:(t + 1) * P, :], x[t % 4][:]).then_inc(stored[t % 4], 16)
                for j in range(4):
                    pool.wait_ge(stored[j], 16 * NT // 4)


class Memory:
    pass


def encoder(nc, a, stop=None, dump=None):
    g = Memory()

    def run(phase):
        with nc.cleanup_on_exit():
            phase(nc, a, g)

    with ExitStack() as ctx:
        allocate(nc, ctx, g)
        with ExitStack() as mix:
            keep = lambda stack, name, shape: stack.enter_context(nc.sbuf_tensor(name, shape, F32))
            g.rkv = keep(mix, "rkv", [P, 3 * HP, T])
            g.lw = keep(mix, "lw", [2 * LORA + 1, T])
            g.la = keep(mix, "la", [2 * LORA + 1, T])
            run(project)
            g.y = keep(mix, "y", [P, HP, T])
            g.upa = keep(mix, "upa", [2 * LORA + 1, 2, HP, P])
            with ExitStack() as rec:
                g.nkk = keep(rec, "nkk", [P, HP, T])
                g.masks = keep(rec, "masks", [P, N_CON_ALL - N_CON])
                g.upw = keep(rec, "upw", [2 * LORA + 1, 2, HP, P])
                g.mk = lambda name: g.masks[:, CON[name][0] - N_CON:CON[name][0] - N_CON + CON[name][1]]
                run(normalise_keys)
                run(scan)
            if stop == "scan":
                dump(nc, g)
                return
            g.conv = keep(mix, "conv2", [P, CT, T])
            g.sg = keep(mix, "sg2", [GLORA, T])
            run(finish_branches)
            run(merge)
        g.gate = ctx.enter_context(nc.sbuf_tensor("gate", [P, 2, E], F32))
        g.index = ctx.enter_context(nc.sbuf_tensor("index", [P, 2, E], U32))
        run(add_and_route)
        run(experts)
        run(final_norm)


def laid_out(inputs):
    f = lambda name: np.asarray(inputs[name])
    x = np.concatenate([f("x_prompt")[0], f("x_sample")[0]], 0)
    col = lambda v, n: v.reshape(n, P).T
    w_in = f("w_in")[0]
    u, gate = RWKV_COLS, RWKV_COLS + 2 * CC
    cols = []
    for j in range(CT):
        cols += [w_in[:, u + P * j:u + P * (j + 1)], w_in[:, u + CC + P * j:u + CC + P * (j + 1)]]
    cols += [w_in[:, gate + P * j:gate + P * (j + 1)] for j in range(2 * KD)]
    cols += [w_in[:, 3 * DR:3 * DR + P],
             np.concatenate([w_in[:, 3 * DR + P:RWKV_COLS], np.zeros((D, P - GLORA), np.float32)], 1)]
    cols += [w_in[:, P * j:P * (j + 1)] for j in range(3 * HP)]
    w_tiles = np.stack([c.reshape(KD, P, P).transpose(1, 0, 2).reshape(P, KD * P) for c in cols])

    def mu(v):
        tail = np.concatenate([v[3 * DR:], np.zeros(P - GLORA, np.float32)])
        return col(np.concatenate([tail, v[:3 * DR]]), 14)

    vec = np.concatenate([
        col(f("norm_mix")[0], KD), mu(f("shift_mu_prev")[0]), mu(f("shift_mu_next")[0]), col(f("k_k")[0], HP),
        col(f("k_a")[0], HP), col(f("r_k")[0].reshape(-1), HP), col(f("lnx_w")[0], HP), col(f("lnx_b")[0], HP),
        col(f("dw_bias")[0], CT), col(f("conv_ln_w")[0], CT), col(f("conv_ln_b")[0], CT),
        f("dw_kernel")[0].reshape(TAPS, CT, P).transpose(2, 1, 0).reshape(P, CT * TAPS)], 1)

    def up(w, bias):
        out = np.zeros((2 * LORA + 1, 2, DR), np.float32)
        for d in range(2):
            out[LORA * d:LORA * (d + 1), d] = w[d]
            out[2 * LORA, d] = bias[d]
        return out.reshape(2 * LORA + 1, 2, HP, P)

    def slabs(w, rows):
        return w.reshape(rows // P, P, KD, P).transpose(2, 1, 0, 3)

    wg, wu, wd = f("exp_w_gate")[0], f("exp_w_up")[0], f("exp_w_down")[0]
    ew = np.empty((E, 12, P, 2048), np.float32)
    for n, w in enumerate((wg, wu)):
        v = w.reshape(E, KD, P, 4, 256).transpose(0, 3, 2, 1, 4).reshape(E, 4, P, 2048)
        ew[:, n:8:2] = v
    ew[:, 8:] = wd.reshape(E, 4, 2, P, D).transpose(0, 1, 3, 2, 4).reshape(E, 4, P, 2048)
    return {
        "x": x, "xT": x.T.reshape(KD, P, T).transpose(1, 0, 2), "w_in": w_tiles, "vec": vec,
        "up_w": up(f("decay_up")[0], f("decay_w0")[0]), "up_a": up(f("iclr_up")[0], f("iclr_a0")[0]),
        "gate_up": f("gate_up")[0],
        "w_o": np.concatenate([slabs(f("w_o_rwkv")[0], DR), slabs(f("w_o_conv")[0], CC)], 2).reshape(KD, P, D),
        "w_out": f("w_out")[0].reshape(KD, P, D).transpose(1, 0, 2),
        "norms": np.stack([f("norm_ffn")[0], f("norm_final")]),
        "router_w": f("router_w")[0].reshape(KD, P, E).transpose(1, 0, 2), "router_b": f("router_b"),
        "ew": ew, "con": constants(),
    }


def kernel(**inputs):
    import concourse.bacc as bacc
    from concourse.bass_utils import run_bass_kernel_spmd

    arrays = {k: np.ascontiguousarray(v) for k, v in laid_out(inputs).items()}
    nc = bacc.Bacc("TRN2", target_bir_lowering=False, num_devices=1)
    a = {k: nc.dram_tensor(f"in_{k}", v.shape, F32, kind="ExternalInput").ap() for k, v in arrays.items()}
    a["out"] = nc.dram_tensor("out", (T, D), F32, kind="ExternalOutput").ap()
    encoder(nc, a)
    r = run_bass_kernel_spmd(nc, [{f"in_{k}": v for k, v in arrays.items()}], core_ids=[0])
    y = r.results[0]["out"]
    return y[:T_PROMPT].reshape(1, T_PROMPT, D), y[T_PROMPT:].reshape(1, T_SAMPLE, D)
```
